# Optimizing a Trainium2 kernel written in Bass

```python
import math
import jax, jax.numpy as jnp
from jax import lax
import numpy as np

D_MODEL = 1024
BATCH = 1
SEQ = 2048
DEPTH = 2
DEC_BATCH = 1
DEC_SEQ = 256
PAST_LEN = 128

N_MIXERS = 2
N_ATTN_LAYERS = (DEPTH + 1) // 2
N_FNET_LAYERS = DEPTH // 2
DA_HEADS = 8
DA_HEAD_DIM = D_MODEL // DA_HEADS // 2
DA_V_DIM = 2 * DA_HEAD_DIM
FN_GROUPS = 8
FN_GROUP_DIM = D_MODEL // FN_GROUPS
Q_BLOCK = 128
EPS = 1e-6
SUBLN_EPS = 1e-5
LAMBDA_STD = 0.1

kernel_name = "diffattn_fnet_interleaved_encoder"

def lambda_init_fn(layer_idx):
    return 0.8 - 0.6 * math.exp(-0.3 * layer_idx)

def rmsnorm(x, g, eps=EPS):
    xf = x.astype(jnp.float32)
    xf = xf * lax.rsqrt(jnp.mean(xf * xf, axis=-1, keepdims=True) + eps)
    return (xf * g.astype(jnp.float32)).astype(x.dtype)

def alibi_slopes(n_heads):
    return 2.0 ** (-(8.0 / n_heads) * jnp.arange(1, n_heads + 1, dtype=jnp.float32))

def diff_attn_branch(h, w_in, w_out, lq1, lk1, lq2, lk2, subln_g, lam_init):
    B, S, D = h.shape
    H, d = DA_HEADS, DA_HEAD_DIM
    proj = h @ w_in
    q, k, v, z = jnp.split(proj, 4, axis=-1)
    q = q.reshape(B, S, H, 2, d).transpose(0, 2, 3, 1, 4)
    k = k.reshape(B, S, H, 2, d).transpose(0, 2, 3, 1, 4)
    v = v.reshape(B, S, H, DA_V_DIM).transpose(0, 2, 1, 3)
    f32 = jnp.float32
    lam = (jnp.exp(jnp.sum(lq1.astype(f32) * lk1.astype(f32)))
           - jnp.exp(jnp.sum(lq2.astype(f32) * lk2.astype(f32))) + lam_init)
    slopes = alibi_slopes(H)
    kpos = jnp.arange(S, dtype=f32)
    scale = d ** -0.5

    def block(start):
        qb = lax.dynamic_slice_in_dim(q, start, Q_BLOCK, axis=3)
        s = jnp.einsum('bhmqd,bhmkd->bhmqk', qb, k,
                       preferred_element_type=f32) * scale
        qpos = start.astype(f32) + jnp.arange(Q_BLOCK, dtype=f32)
        dist = jnp.abs(qpos[:, None] - kpos[None, :])
        s = s - (slopes[:, None, None] * dist)[None, :, None]
        p = jax.nn.softmax(s, axis=-1)
        pd = p[:, :, 0] - lam * p[:, :, 1]
        return jnp.einsum('bhqk,bhkv->bhqv', pd.astype(v.dtype), v)

    starts = jnp.arange(S // Q_BLOCK, dtype=jnp.int32) * Q_BLOCK
    o = lax.map(block, starts)
    o = o.transpose(1, 0, 3, 2, 4).reshape(B, S, H, DA_V_DIM)
    o = rmsnorm(o, subln_g, SUBLN_EPS) * (1.0 - lam_init)
    o = o.reshape(B, S, D) * jax.nn.silu(z)
    return o @ w_out

def fourier_branch(h, w_in, w_out):
    B, S, D = h.shape
    u, z = jnp.split(h @ w_in, 2, axis=-1)
    ug = u.astype(jnp.float32).reshape(B, S, FN_GROUPS, FN_GROUP_DIM)
    f = jnp.fft.fft2(ug, axes=(1, 3), norm="ortho").real
    f = f.reshape(B, S, D).astype(h.dtype)
    return (f * jax.nn.silu(z)) @ w_out

def trunk(x, attn_norm, attn_w_in, attn_lambda_q1, attn_lambda_k1, attn_lambda_q2,
          attn_lambda_k2, attn_subln, attn_w_out, fnet_norm, fnet_w_in, fnet_w_out, final_norm):
    for i in range(DEPTH):
        j = i // N_MIXERS
        if i % N_MIXERS == 0:
            h = rmsnorm(x, attn_norm[j])
            x = x + diff_attn_branch(h, attn_w_in[j], attn_w_out[j], attn_lambda_q1[j],
                                     attn_lambda_k1[j], attn_lambda_q2[j], attn_lambda_k2[j],
                                     attn_subln[j], lambda_init_fn(i))
        else:
            h = rmsnorm(x, fnet_norm[j])
            x = x + fourier_branch(h, fnet_w_in[j], fnet_w_out[j])
    return rmsnorm(x, final_norm)

def setup_inputs(seed: int = 0) -> dict:
    key = jax.random.key(seed)
    ks = jax.random.split(key, 16)
    D = D_MODEL
    na, nf = N_ATTN_LAYERS, N_FNET_LAYERS
    nrm = jax.random.normal
    return {
        "x_prompt": nrm(ks[0], (BATCH, SEQ, D), jnp.float32),
        "x_sample": nrm(ks[1], (DEC_BATCH, DEC_SEQ, D), jnp.float32),
        "attn_norm": 1.0 + 0.01 * nrm(ks[2], (na, D), jnp.float32),
        "attn_w_in": nrm(ks[3], (na, D, 4 * D), jnp.float32) * D ** -0.5,
        "attn_lambda_q1": LAMBDA_STD * nrm(ks[4], (na, DA_HEAD_DIM), jnp.float32),
        "attn_lambda_k1": LAMBDA_STD * nrm(ks[5], (na, DA_HEAD_DIM), jnp.float32),
        "attn_lambda_q2": LAMBDA_STD * nrm(ks[6], (na, DA_HEAD_DIM), jnp.float32),
        "attn_lambda_k2": LAMBDA_STD * nrm(ks[7], (na, DA_HEAD_DIM), jnp.float32),
        "attn_subln": 1.0 + 0.01 * nrm(ks[8], (na, DA_V_DIM), jnp.float32),
        "attn_w_out": nrm(ks[9], (na, D, D), jnp.float32) * D ** -0.5,
        "fnet_norm": 1.0 + 0.01 * nrm(ks[10], (nf, D), jnp.float32),
        "fnet_w_in": nrm(ks[11], (nf, D, 2 * D), jnp.float32) * D ** -0.5,
        "fnet_w_out": nrm(ks[12], (nf, D, D), jnp.float32) * D ** -0.5,
        "final_norm": 1.0 + 0.01 * nrm(ks[13], (D,), jnp.float32),
    }

def reference(x_prompt, x_sample, attn_norm, attn_w_in, attn_lambda_q1, attn_lambda_k1,
              attn_lambda_q2, attn_lambda_k2, attn_subln, attn_w_out, fnet_norm, fnet_w_in,
              fnet_w_out, final_norm):
    y_prompt = trunk(x_prompt, attn_norm, attn_w_in, attn_lambda_q1, attn_lambda_k1,
                     attn_lambda_q2, attn_lambda_k2, attn_subln, attn_w_out, fnet_norm,
                     fnet_w_in, fnet_w_out, final_norm)
    y_sample = trunk(x_sample, attn_norm, attn_w_in, attn_lambda_q1, attn_lambda_k1,
                     attn_lambda_q2, attn_lambda_k2, attn_subln, attn_w_out, fnet_norm,
                     fnet_w_in, fnet_w_out, final_norm)
    return (y_prompt, y_sample)


_drawn_inputs = setup_inputs


def setup_inputs(seed=0):
    import zlib

    import numpy as np

    out = dict(_drawn_inputs(seed))
    spreads = {}
    factors = {'attn_norm': 5.878,
     'attn_lambda_k1': 3.78,
     'attn_lambda_q2': 3.988,
     'attn_subln': 8.0,
     'fnet_norm': 8.0,
     'final_norm': 5.483}
    for name, (base, spread) in spreads.items():
        noise = np.random.default_rng([zlib.crc32(name.encode()), seed]).standard_normal(out[name].shape)
        drawn = base * np.exp(spread * noise) if base else spread * noise
        out[name] = __import__('jax').numpy.asarray(drawn.astype(out[name].dtype))
    for name, factor in factors.items():
        out[name] = (out[name] * factor).astype(out[name].dtype)
    return out
```

```python
import math
from contextlib import ExitStack

import numpy as np

import concourse.bass as bass
from concourse import mybir

F32 = mybir.dt.float32
F32R = mybir.dt.float32r
ALU = mybir.AluOpType
ACT = mybir.ActivationFunctionType
AX_X = mybir.AxisListType.X

P = 128
D = 1024
KB = D // P
S_PROMPT, S_SAMPLE = 2048, 256
T = S_PROMPT + S_SAMPLE
HEADS = 8
HD = 64
GROUP = 512
GROUPS = [(t, min(GROUP, T - t)) for t in range(0, T, GROUP)]
NG = len(GROUPS)
NT = T // P
EPS = 1e-6
SUBLN_EPS = 1e-5
LAM_INIT = 0.8 - 0.6 * math.exp(-0.3 * 0)
SCALE = HD ** -0.5
ALIBI = 32


def wait(eng, sem, value):
    if not (isinstance(value, int) and value <= 0):
        eng.wait_ge(sem, value)


def hold(eng, held, sem, value):
    eng.wait_ge(sem, value)
    eng.sem_inc(held, 1)


def f32(ap):
    return ap.bitcast(F32)


class Memory:

    def __init__(self, nc, stack, tag):
        self.nc, self.tag = nc, tag
        self.stack = stack.enter_context(ExitStack())
        self.sems = []
        stack.callback(self.clear)

    def sb(self, name, shape, dt=F32):
        return self.stack.enter_context(self.nc.sbuf_tensor(f"{self.tag}_{name}", shape, dt))

    def ps(self, name, shape, dt=F32):
        return self.stack.enter_context(self.nc.psum_tensor(f"{self.tag}_{name}", shape, dt))

    def sem(self, name):
        self.sems.append(self.nc.alloc_semaphore(f"{self.tag}_{name}"))
        return self.sems[-1]

    def clear(self):
        self.nc.clear_and_free_semaphores(self.sems)
        self.nc.all_engine_barrier()



def alibi_constants():
    nb = S_PROMPT // P
    slope = 2.0 ** -np.arange(1, HEADS + 1) / SCALE
    t = np.arange(S_PROMPT)
    sign = np.sign(np.arange(nb)[:, None] - t[None, :] // P)
    gap = P * np.abs(np.arange(nb)[:, None] - t[None, :] // P)
    penalty = np.concatenate([gap - sign * (t % P), sign])[None] * -slope[:, None, None]
    mine = np.arange(nb)[:, None] == t[None, :] // P
    a = np.arange(P)
    return {"ident": np.eye(P, dtype=np.float32),
            "position": np.concatenate([mine, mine * (t % P)]).astype(np.float32),
            "penalty": penalty.astype(np.float32),
            "diag": (-slope[:, None, None] * np.abs(a[:, None] - a[None, :])[None]).astype(np.float32)}



def three_pass(pe, out, a_hi, a_lo, b_hi, b_lo, ks, first=True, last=True):
    mm = None
    for n, k in enumerate(ks):
        pe.matmul(out, a_hi(k), b_hi(k), start=first and n == 0, stop=False)
        pe.matmul(out, a_hi(k), b_lo(k), start=False, stop=False)
        mm = pe.matmul(out, a_lo(k), b_hi(k), start=False, stop=last and n == len(ks) - 1)
    return mm



def project_resident(nc, tag, w_dram, norm_dram, ident_dram, sections, source, spill=None):
    rows = source[0] == "rows"
    with ExitStack() as stack:
        m = Memory(nc, stack, tag)
        xh = m.sb("xh", [P, KB, T], F32R)
        xl = m.sb("xl", [P, KB, T], F32R)
        rstd = m.sb("rstd", [P, T])
        raw = m.sb("raw", [P, KB, P])
        wg = m.sb("wg", [P, KB, P])
        wh = m.sb("wh", [P, 2, KB, P], F32R)
        wl = m.sb("wl", [P, 2, KB, P], F32R)
        stage = m.sb("stage", [P, 6, GROUP])
        norm_w = m.sb("norm_w", [P, KB])
        ones = m.sb("ones", [P, P])
        eps = m.sb("eps", [P, 1])
        xr = m.sb("xr", [P, 2, D])
        ident = m.sb("ident", [P, P])
        acc = m.ps("acc", [P, 8, GROUP])

        norm_in = m.sem("norm_in")
        ident_in = m.sem("ident_in")
        consts_set = m.sem("consts_set")
        x_in = [m.sem(f"x_in{s}") for s in range(2)]
        transposed = m.sem("transposed")
        x_hi = m.sem("x_hi")
        squared = m.sem("squared")
        x_lo = m.sem("x_lo")
        tile_sums = m.sem("tile_sums")
        sums = m.sem("sums")
        rooted = m.sem("rooted")
        rstd_done = m.sem("rstd_done")
        raw_in = m.sem("raw_in")
        wg_done = m.sem("wg_done")
        w_hi = m.sem("w_hi")
        w_lo = m.sem("w_lo")
        products = m.sem("products")
        scaled = m.sem("scaled")
        out_hi = m.sem("out_hi")
        out_lo = m.sem("out_lo")
        stored = [m.sem(f"stored{s}") for s in range(2)]
        spilled = m.sem("spilled")
        all_blocks = sum(n for n, _, _ in sections)

        def square(s):
            return stage[:, 2 * s:2 * s + 2, :].rearrange("p a b -> p (a b)")

        def x_tile(s):
            if rows:
                return acc[:, 2 * s:2 * s + 2, :].rearrange("p a (b t) -> p (a b) t", t=P)
            return xr[:, s].rearrange("p (k t) -> p k t", k=KB)

        def x_arrived(eng, s, j):
            if rows:
                eng.wait_ge(transposed, 2 * j + s + 3)
            else:
                eng.wait_ge(x_in[s], 16 * j + 16)

        def units(eng):
            blocks0 = his = los = 0
            stores = 0
            for blocks, kind, dest in sections:
                per = 32 if kind == "split" else 16
                with eng.Fori(0, blocks // 2) as j:
                    for v in range(2 * NG):
                        u, g = divmod(v, NG)
                        yield (2 * NG * j + v + NG * blocks0, 2 * j + u, blocks0, u, g, v % 2, kind, dest,
                               2 * NG * j + v + his, 2 * NG * j + v + los,
                               per * (NG * j + v // 2) + stores)
                blocks0 += blocks
                his += NG * blocks if kind != "plain" else 0
                los += NG * blocks if kind == "split" else 0
                stores += per * NG * blocks // 2
            units.stores = stores

        with nc.Block() as block:
            @block.sync
            def _(sp):
                sp.dma_start(norm_w[:], norm_dram).then_inc(norm_in, 16)
                sp.dma_start(ident[:], ident_dram).then_inc(ident_in, 16)

                def load(j, x):
                    for s in range(2):
                        t = 2 * j + s
                        if rows:
                            sp.wait_ge(transposed, t + 1)
                            sp.dma_start(xr[:, s], x(t)).then_inc(x_in[s], 16)
                        else:
                            sp.wait_ge(x_lo, t + 1)
                            sp.dma_start(x_tile(s), x(t)).then_inc(x_in[s], 16)
                if rows:
                    with sp.Fori(0, S_PROMPT // P // 2) as j:
                        load(j, lambda t: source[1][bass.ds(t * P, P), :])
                    load(S_PROMPT // P // 2, lambda t: source[2][t * P - S_PROMPT:t * P - S_PROMPT + P, :])
                    sp.wait_ge(x_lo, NT + 2)
                    sp.dma_start(spill[0].rearrange("k p t -> p k t"), f32(xh[:])).then_inc(spilled, 16)
                    sp.dma_start(spill[1].rearrange("k p t -> p k t"), f32(xl[:])).then_inc(spilled, 16)
                else:
                    with sp.Fori(0, NT // 2) as j:
                        load(j, lambda t: source[1].rearrange("k p t -> p k t")[:, :, bass.ds(t * P, P)])
                for unit, blk, blocks0, u, g, s, kind, dest, hi_n, lo_n, _ in units(sp):
                    t0, n = GROUPS[g]
                    if kind == "plain":
                        sp.wait_ge(scaled, unit + 1 + NG)
                        sp.dma_start(dest[0][bass.ds(blk, 1), :, t0:t0 + n].rearrange("a p t -> p (a t)"),
                                     stage[:, s, :n]).then_inc(stored[s], 16)
                    else:
                        sp.wait_ge(out_hi, hi_n + 1)
                        sp.dma_start(dest[0][bass.ds(blk, 1), :, t0:t0 + n].rearrange("a p t -> p (a t)"),
                                     stage[:, 2 + s, :n]).then_inc(stored[s], 16)
                    if kind == "split":
                        sp.wait_ge(out_lo, lo_n + 1)
                        sp.dma_start(dest[1][bass.ds(blk, 1), :, t0:t0 + n].rearrange("a p t -> p (a t)"),
                                     stage[:, 4 + s, :n]).then_inc(stored[s], 16)
                for s in range(2):
                    sp.wait_ge(stored[s], units.stores)
                if rows:
                    sp.wait_ge(spilled, 32)

            @block.gpsimd
            def _(pool):
                w_view = w_dram.rearrange("a (k p) n -> p (a k) n", p=P)
                pool.wait_ge(norm_in, 16)
                with pool.Fori(0, all_blocks // 2) as j:
                    for u in range(2):
                        b = 2 * j + u
                        pool.wait_ge(wg_done, b)
                        pool.dma_start(raw[:], w_view[:, :, bass.ds(b * P, P)]).then_inc(raw_in, 16)
                        pool.wait_ge(raw_in, 16 * b + 16)
                        pool.wait_ge(products, NG * b)
                        norm_b = norm_w[:, :, None].to_broadcast([P, KB, P])
                        pool.tensor_tensor(wh[:, u], raw[:], norm_b, ALU.mult).then_inc(w_hi, 1)
                        pool.wait_ge(w_lo, b)
                        pool.tensor_tensor(wg[:], raw[:], norm_b, ALU.mult).then_inc(wg_done, 1)
                        pool.wait_ge(w_hi, b + 1)
                        pool.wait_ge(wg_done, b + 1)
                        pool.tensor_tensor(wl[:, u], wg[:], f32(wh[:, u]), ALU.subtract).then_inc(w_lo, 1)

            @block.tensor
            def _(pe):
                pe.sem_inc(products, NG)
                pe.sem_inc(transposed, 2)
                pe.wait_ge(ident_in, 16)
                pe.wait_ge(consts_set, 2)
                if rows:
                    with pe.Fori(0, NT // 2) as j:
                        for s in range(2):
                            t = 2 * j + s
                            pe.wait_ge(x_in[s], 16 * j + 16)
                            pe.wait_ge(x_lo, t + 1)
                            for k in range(KB):
                                mm = pe.transpose(acc[:, 2 * s + k // 4, (k % 4) * P:(k % 4 + 1) * P],
                                                  xr[:, s, k * P:(k + 1) * P], ident[:])
                            mm.then_inc(transposed, 1)
                for g, (t0, n) in enumerate(GROUPS):
                    pe.wait_ge(tile_sums, (t0 + n) // P + 2)
                    wait(pe, rooted, g - 1)
                    pe.matmul(acc[:, 5 + g % 2, :n], ones[:], rstd[:, t0:t0 + n],
                              start=True, stop=True).then_inc(sums, 1)
                pe.wait_ge(x_lo, NT + 2)
                for unit, blk, blocks0, u, g, s, kind, dest, _, _, _ in units(pe):
                    t0, n = GROUPS[g]
                    if g == 0:
                        pe.wait_ge(w_lo, blk + blocks0 + 1)
                    pe.wait_ge(scaled, unit + 1)
                    three_pass(pe, acc[:, g, :n], lambda k: wh[:, u, k], lambda k: wl[:, u, k],
                               lambda k: xh[:, k, t0:t0 + n], lambda k: xl[:, k, t0:t0 + n],
                               range(KB)).then_inc(products, 1)

            @block.scalar
            def _(act):
                act.wait_ge(consts_set, 2)
                with act.Fori(0, NT // 2) as j:
                    for s in range(2):
                        t = 2 * j + s
                        x_arrived(act, s, j)
                        act.activation(xh[:, :, bass.ds(t * P, P)], x_tile(s), ACT.Copy).then_inc(x_hi, 1)
                        act.wait_ge(tile_sums, t + 1)
                        act.activation(square(s).rearrange("p (k t) -> p k t", k=KB), x_tile(s),
                                       ACT.Square).then_inc(squared, 1)
                for g, (t0, n) in enumerate(GROUPS):
                    act.wait_ge(sums, g + 1)
                    act.activation(rstd[:, t0:t0 + n], acc[:, 5 + g % 2, :n], ACT.Sqrt,
                                   bias=eps[:, 0:1], scale=1.0 / D).then_inc(rooted, 1)
                for unit, blk, blocks0, u, g, s, kind, dest, hi_n, _, slot_stores in units(act):
                    t0, n = GROUPS[g]
                    if kind == "plain":
                        continue
                    act.wait_ge(scaled, unit + 1 + NG)
                    act.wait_ge(stored[s], slot_stores)
                    out = stage[:, 2 + s, :n]
                    act.activation(out.bitcast(F32R) if kind == "split" else out, stage[:, s, :n],
                                   ACT.Copy if kind == "split" else ACT.Silu).then_inc(out_hi, 1)

            @block.vector
            def _(dve):
                dve.sem_inc(x_lo, 2)
                dve.sem_inc(tile_sums, 2)
                dve.sem_inc(scaled, NG)
                dve.memset(ones[:], 1.0).then_inc(consts_set, 1)
                dve.memset(eps[:], EPS).then_inc(consts_set, 1)
                with dve.Fori(0, NT // 2) as j:
                    for s in range(2):
                        t = 2 * j + s
                        dve.wait_ge(squared, t + 1)
                        dve.tensor_tensor(xl[:, :, bass.ds(t * P, P)], x_tile(s),
                                          f32(xh[:, :, bass.ds(t * P, P)]), ALU.subtract).then_inc(x_lo, 1)
                        dve.tensor_reduce(rstd[:, bass.ds(t * P, P)],
                                          square(s).rearrange("p (k t) -> p t k", k=KB),
                                          AX_X, ALU.add).then_inc(tile_sums, 1)
                for g, (t0, n) in enumerate(GROUPS):
                    dve.wait_ge(rooted, g + 1)
                    dve.reciprocal(rstd[:, t0:t0 + n], rstd[:, t0:t0 + n]).then_inc(rstd_done, 1)
                dve.wait_ge(rstd_done, NG)
                for unit, blk, blocks0, u, g, s, kind, dest, hi_n, lo_n, slot_stores in units(dve):
                    t0, n = GROUPS[g]
                    dve.wait_ge(products, unit + 1 + NG)
                    dve.wait_ge(stored[s], slot_stores)
                    dve.tensor_tensor(stage[:, s, :n], acc[:, g, :n], rstd[:, t0:t0 + n],
                                      ALU.mult).then_inc(scaled, 1)
                    if kind == "split":
                        dve.wait_ge(out_hi, hi_n + 1)
                        dve.tensor_tensor(stage[:, 4 + s, :n].bitcast(F32R), stage[:, s, :n],
                                          stage[:, 2 + s, :n], ALU.subtract).then_inc(out_lo, 1)



def load_lambda(m, sp_sem):
    return dict(vec=m.sb("lam_vec", [P, 4, HD]), prod=m.sb("lam_prod", [P, 2, HD]),
                dot=m.sb("lam_dot", [P, 2]), exps=m.sb("lam_exps", [P, 2]), neg=m.sb("lam_neg", [P, 1]),
                loaded=sp_sem, dotted=m.sem("lam_dotted"), exped=m.sem("lam_exped"), done=m.sem("lam_done"))


def lambda_load(sp, lam, vectors):
    for n, v in enumerate(vectors):
        sp.dma_start(lam["vec"][:, n], v.to_broadcast([P, HD])).then_inc(lam["loaded"], 16)


def lambda_dots(dve, lam):
    dve.wait_ge(lam["loaded"], 64)
    dve.tensor_tensor(lam["prod"][:], lam["vec"][:, 0::2], lam["vec"][:, 1::2], ALU.mult).then_inc(lam["dotted"], 1)
    dve.wait_ge(lam["dotted"], 1)
    dve.tensor_reduce(lam["dot"][:], lam["prod"][:], AX_X, ALU.add).then_inc(lam["dotted"], 1)


def lambda_exps(act, lam):
    act.wait_ge(lam["dotted"], 2)
    act.activation(lam["exps"][:], lam["dot"][:], ACT.Exp).then_inc(lam["exped"], 1)


def lambda_negative(dve, lam):
    dve.wait_ge(lam["exped"], 1)
    dve.tensor_tensor(lam["neg"][:], lam["exps"][:, 1:2], lam["exps"][:, 0:1], ALU.subtract).then_inc(lam["done"], 1)
    dve.wait_ge(lam["done"], 1)
    dve.tensor_scalar(lam["neg"][:], lam["neg"][:], LAM_INIT, None, ALU.subtract).then_inc(lam["done"], 1)


def attend_prompt(nc, qk_hi, qk_lo, v_dram, o_dram, consts, lam_vectors):
    S, NB = S_PROMPT, S_PROMPT // P
    PAIR = 2 * P
    NP = NB // 2
    NC = NB // 4
    UNITS = 4 * NB + NC
    with ExitStack() as stack:
        m = Memory(nc, stack, "pa")
        ka = m.sb("ka", [P, 2, S], F32R)
        kb = m.sb("kb", [HD + ALIBI, 2, S], F32R)
        qa = m.sb("qa", [P, 2, 2, PAIR], F32R)
        qb = m.sb("qb", [HD + ALIBI, 2, 2, PAIR], F32R)
        diag = m.sb("diag", [P, 2, P], F32R)
        vt = m.sb("vt", [P, S])
        vh = m.sb("vh", [P, NB, P], F32R)
        vl = m.sb("vl", [P, NB, P], F32R)
        p0 = m.sb("p0", [P, 4, S])
        p1 = m.sb("p1", [P, 2, S])
        wth = m.sb("wth", [P, 2, NB, PAIR], F32R)
        wtl = m.sb("wtl", [P, 2, NB, PAIR], F32R)
        o_out = m.sb("o_out", [P, 2, PAIR])
        half_max = m.sb("half_max", [P, 2, 2, 2])
        neg_max = m.sb("neg_max", [P, 2, 2])
        half_sum = m.sb("half_sum", [P, 2, 2, 2])
        row_sum = m.sb("row_sum", [P, 2, 2])
        inv_sum = m.sb("inv_sum", [P, 2, 2])
        ident = m.sb("ident", [P, P])
        ident_r = m.sb("ident_r", [P, P], F32R)
        score = m.ps("score", [P, NC, GROUP])
        turned = m.ps("turned", [P, 3, GROUP])
        o_acc = m.ps("o_acc", [P, PAIR])

        consts_in = m.sem("consts_in")
        k_in = [m.sem(f"k_in{n}") for n in range(2)]
        q_in = [m.sem(f"q_in{n}") for n in range(2)]
        v_in = m.sem("v_in")
        scores = m.sem("scores")
        halves_max = m.sem("halves_max")
        maxima = m.sem("maxima")
        exps = m.sem("exps")
        row_sums = m.sem("row_sums")
        inverses = m.sem("inverses")
        p1_scaled = m.sem("p1_scaled")
        weights = m.sem("weights")
        turns = m.sem("turns")
        turned_hi = m.sem("turned_hi")
        turned_lo = m.sem("turned_lo")
        pair_done = m.sem("pair_done")
        o_copied = m.sem("o_copied")
        o_stored = [m.sem(f"o_stored{n}") for n in range(2)]
        pool_held, sp_held = m.sem("pool_held"), m.sem("sp_held")
        lam = load_lambda(m, m.sem("lam_in"))

        order = []
        for q in range(NB):
            order += [(q, "w", c) for c in range(NC)]
            if q in (2, 3):
                order += [(q, "v", 2 * (q - 2) + c) for c in range(2)]
        assert len(order) == UNITS
        place = {x: n for n, x in enumerate(order)}
        SKIPPED = 2 * NC

        def unit(h, q, kind, c):
            n = place[(q, kind, c)]
            return UNITS * h + n - SKIPPED, n % 3, n

        def step_parts(h, q):
            first = isinstance(h, int) and h == 0
            return dict(score=not (isinstance(h, int) and h == HEADS),
                        before=not (first and q == 0), weights=not (first and q < 2),
                        pairs=not (first and q < 4), out=q % 2 == 0 and not (first and q < 6))

        def run(eng, step, heads=HEADS, tail=5):
            for q in range(NB):
                step(0, q)
            with eng.Fori(1, heads) as h:
                for q in range(NB):
                    step(h, q)
            for q in range(tail):
                step(heads, q)

        with nc.Block() as block:
            @block.sync
            def _(sp):
                sp.dma_start(ident[:], consts["ident"]).then_inc(consts_in, 16)
                sp.dma_start(f32(ident_r[:]), consts["ident"]).then_inc(consts_in, 16)
                for n in range(2):
                    sp.dma_start(f32(kb[HD:, n]), consts["position"]).then_inc(consts_in, 16)

                def row(src, h, at, rows, t0, n):
                    return src[bass.ds(h, 1), at:at + rows, t0:t0 + n].rearrange("a p t -> p (a t)")

                def load_k(h, n):
                    sp.dma_start(f32(ka[0:HD, n]), row(qk_hi, HEADS + h, HD * n, HD, 0, S)).then_inc(k_in[n], 16)
                    sp.dma_start(f32(ka[HD:P, n]), row(qk_hi, HEADS + h, HD * n, HD, 0, S)).then_inc(k_in[n], 16)
                    sp.dma_start(f32(kb[0:HD, n]), row(qk_lo, HEADS + h, HD * n, HD, 0, S)).then_inc(k_in[n], 16)

                def load_q(h, g):
                    s, t0 = g % 2, g * PAIR
                    for n in range(2):
                        hi = row(qk_hi, h, HD * n, HD, t0, PAIR)
                        sp.dma_start(f32(qa[0:HD, s, n]), hi).then_inc(q_in[s], 16)
                        sp.dma_start(f32(qa[HD:P, s, n]), row(qk_lo, h, HD * n, HD, t0, PAIR)).then_inc(q_in[s], 16)
                        sp.dma_start(f32(qb[0:HD, s, n]), hi).then_inc(q_in[s], 16)
                        sp.dma_start(f32(qb[HD:, s, n]), row(consts["penalty"], h, 0, ALIBI, t0, PAIR)).then_inc(q_in[s], 16)
                    sp.dma_start(f32(diag[:, s]), row(consts["diag"], h, 0, P, 0, P)).then_inc(q_in[s], 16)

                def load_v(h):
                    sp.dma_start(vt[:], row(v_dram, h, 0, P, 0, S)).then_inc(v_in, 16)

                load_q(0, 0)
                for n in range(2):
                    load_k(0, n)
                load_v(0)
                lambda_load(sp, lam, lam_vectors)


                def step(h, q, follows):
                    parts = step_parts(h, q)
                    i = NB * h + q
                    if parts["score"] and q % 2 == 0 and (q + 2 < NB or follows):
                        if not (isinstance(i, int) and i == 0):
                            hold(sp, sp_held, scores, 4 * i)
                        nxt = q // 2 + 1
                        load_q(h, nxt) if nxt < NP else load_q(h + 1, 0)
                    if parts["out"]:
                        g = NP * h + q // 2 - 3
                        hold(sp, sp_held, o_copied, g + 1)
                        s = (q // 2 - 3) % 2
                        prev, t0 = (h, (q // 2 - 3) * PAIR) if q >= 6 else (h - 1, (q // 2 - 3 + NP) * PAIR)
                        sp.dma_start(row(o_dram, prev, 0, P, t0, PAIR), o_out[:, s]).then_inc(o_stored[s], 16)
                    if follows and q == 4:
                        hold(sp, sp_held, turns, unit(h, 3, "v", NC - 1)[0] + 1)
                        load_v(h + 1)
                    if follows and q == NB - 1:
                        for n in range(2):
                            hold(sp, sp_held, scores, 4 * i + 2 * n + 2)
                            load_k(h + 1, n)

                for q in range(NB):
                    step(0, q, True)
                with sp.Fori(1, HEADS - 1) as h:
                    for q in range(NB):
                        step(h, q, True)
                for q in range(NB):
                    step(HEADS - 1, q, False)
                for q in range(5):
                    step(HEADS, q, False)
                for s in range(2):
                    sp.wait_ge(o_stored[s], 16 * HEADS * NP // 2)

            @block.tensor
            def _(pe):
                pe.wait_ge(consts_in, 64)

                def score_map(h, q, n):
                    i = NB * h + q
                    s, at = (q // 2) % 2, (q % 2) * P
                    if n == 0 and q % 2 == 0:
                        pe.wait_ge(q_in[s], 144 * (NP // 2 * h + q // 4 + 1))
                    if q == 0:
                        pe.wait_ge(k_in[n], 48 * (h + 1))
                    for c in range(NC):
                        if c % 2 == 0:
                            wait(pe, exps, 4 * i + 2 * n + c // 2 - 1)
                        mine = q // 4 == c
                        cols = slice(c * GROUP, (c + 1) * GROUP)
                        pe.matmul(score[:, c], qa[:, s, n, at:at + P], ka[:, n, cols], start=True, stop=False)
                        if mine:
                            k0 = (q % 4) * P
                            pe.matmul(score[:, c, k0:k0 + P], ident_r[:], diag[:, s], start=False, stop=False)
                        mm = pe.matmul(score[:, c], qb[:, s, n, at:at + P], kb[:, n, cols],
                                       start=False, stop=True)
                        if c % 2 == 1:
                            mm.then_inc(scores, 1)

                def bank_free(u, n, h):
                    wait(pe, turned_lo, u - 2 if n >= 3 else u - n)

                def turn_weights(h, q):
                    i = NB * h + q - 2
                    pe.wait_ge(weights, i + 1)
                    for c in range(NC):
                        u, b, n = unit(h, q, "w", c)
                        bank_free(u, n, h)
                        for x in range(4):
                            k = 4 * c + x
                            mm = pe.transpose(turned[:, b, x * P:(x + 1) * P],
                                              p0[:, (q - 2) % 4, k * P:(k + 1) * P], ident[:])
                        mm.then_inc(turns, 1)

                def turn_v(h, q, c):
                    u, b, n = unit(h, q, "v", c)
                    pe.wait_ge(v_in, 16 * (h + 1))
                    bank_free(u, n, h)
                    for x in range(4):
                        k = 4 * c + x
                        mm = pe.transpose(turned[:, b, x * P:(x + 1) * P], vt[:, k * P:(k + 1) * P], ident[:])
                    mm.then_inc(turns, 1)

                def pair_product(h, q, part):
                    g = NP * h + q // 2 - 2
                    s = (q // 2) % 2
                    c = 2 * (q % 2) + part
                    if c == 0:
                        last = unit(h, q - 1, "w", NC - 1) if q else None
                        pe.wait_ge(turned_lo, last[0] + 1 if q else UNITS * h - SKIPPED)
                        wait(pe, o_copied, g)
                    if q >= 4 and q < 6:
                        vq = 2 + c // 2
                        pe.wait_ge(turned_lo, unit(h, vq, "v", c)[0] + 1)
                    mm = three_pass(pe, o_acc[:], lambda k: vh[:, k], lambda k: vl[:, k],
                                    lambda k: wth[:, s, k], lambda k: wtl[:, s, k],
                                    range(4 * c, 4 * c + 4), first=c == 0, last=c == NC - 1)
                    if c == NC - 1:
                        mm.then_inc(pair_done, 1)

                def step(h, q):
                    parts = step_parts(h, q)
                    if parts["score"]:
                        score_map(h, q, 0)
                    if parts["weights"] and (parts["score"] or q < 2):
                        turn_weights(h, q)
                    if parts["score"]:
                        score_map(h, q, 1)
                    for part in range(2):
                        if parts["pairs"] and (parts["score"] or q < 4):
                            pair_product(h, q, part)
                        if parts["score"] and q in (2, 3):
                            turn_v(h, q, 2 * (q - 2) + part)
                run(pe, step)

            @block.scalar
            def _(act):
                lambda_exps(act, lam)

                def take_hi(h, q, kind, c):
                    u, b, _ = unit(h, q, kind, c)
                    act.wait_ge(turns, u + 1)
                    src = turned[:, b].rearrange("p (k t) -> p k t", k=4)
                    if kind == "w":
                        s, at = ((q - 2) // 2) % 2, (q % 2) * P
                        out = wth[:, s, 4 * c:4 * c + 4, at:at + P]
                    else:
                        out = vh[:, 4 * c:4 * c + 4]
                    act.activation(out, src, ACT.Copy).then_inc(turned_hi, 1)

                def exponentials(h, q, n):
                    i = NB * h + q
                    act.wait_ge(maxima, 2 * i + n + 1)
                    if n == 0:
                        if not (isinstance(h, int) and h == 0 and q < 4):
                            if q >= 2:
                                act.wait_ge(turns, unit(h, q - 2, "w", NC - 1)[0] + 1) if q >= 2 else None
                            else:
                                act.wait_ge(turns, unit(h, NB - 2 + q, "w", NC - 1)[0] - UNITS + 1)
                    else:
                        wait(act, weights, i - 1)
                    dst = p0[:, q % 4] if n == 0 else p1[:, q % 2]
                    for half in range(2):
                        act.activation(dst[:, half * S // 2:(half + 1) * S // 2],
                                       score[:, 2 * half:2 * half + 2].rearrange("p a b -> p (a b)"), ACT.Exp,
                                       bias=neg_max[:, q % 2, n:n + 1], scale=SCALE,
                                       accum_out=half_sum[:, q % 2, n, half:half + 1]).then_inc(exps, 1)

                def step(h, q):
                    parts = step_parts(h, q)
                    w = parts["weights"] and (parts["score"] or q < 2)
                    for c in range(3 if w else 0):
                        take_hi(h, q, "w", c)
                    if parts["score"]:
                        exponentials(h, q, 0)
                    if w:
                        take_hi(h, q, "w", 3)
                    if parts["out"]:
                        g = NP * h + q // 2 - 3
                        s = (q // 2 - 3) % 2
                        act.wait_ge(pair_done, g + 1)
                        wait(act, o_stored[s], 16 * (NP // 2 * h + (q // 2 - 3) // 2))
                        act.activation(o_out[:, s], o_acc[:], ACT.Copy).then_inc(o_copied, 1)
                    if parts["score"]:
                        exponentials(h, q, 1)
                        if q in (2, 3):
                            for part in range(2):
                                take_hi(h, q, "v", 2 * (q - 2) + part)
                run(act, step)

            @block.vector
            def _(dve):
                lambda_dots(dve, lam)
                lambda_negative(dve, lam)

                def maximum(h, q, n):
                    i = NB * h + q
                    for half in range(2):
                        dve.wait_ge(scores, 4 * i + 2 * n + half + 1)
                        dve.tensor_reduce(half_max[:, q % 2, n, half:half + 1],
                                          score[:, 2 * half:2 * half + 2].rearrange("p a b -> p (a b)"),
                                          AX_X, ALU.max).then_inc(halves_max, 1)
                    dve.wait_ge(halves_max, 4 * i + 2 * n + 2)
                    dve.tensor_scalar(neg_max[:, q % 2, n:n + 1], half_max[:, q % 2, n, 0:1],
                                      half_max[:, q % 2, n, 1:2], -SCALE, ALU.max, ALU.mult).then_inc(maxima, 1)

                def inverse_sums(h, q, i, par):
                    dve.wait_ge(exps, 4 * i + 4)
                    dve.tensor_tensor(row_sum[:, par], half_sum[:, par, :, 0], half_sum[:, par, :, 1],
                                      ALU.add).then_inc(row_sums, 1)
                    dve.wait_ge(row_sums, i + 1)
                    dve.reciprocal(inv_sum[:, par], row_sum[:, par]).then_inc(inverses, 1)

                def take_lo(h, q, kind, c):
                    u, b, _ = unit(h, q, kind, c)
                    dve.wait_ge(turned_hi, u + 1)
                    src = turned[:, b].rearrange("p (k t) -> p k t", k=4)
                    if kind == "w":
                        s, at = ((q - 2) // 2) % 2, (q % 2) * P
                        hi, out = (x[:, s, 4 * c:4 * c + 4, at:at + P] for x in (wth, wtl))
                    else:
                        hi, out = (x[:, 4 * c:4 * c + 4] for x in (vh, vl))
                    dve.tensor_tensor(out, src, f32(hi), ALU.subtract).then_inc(turned_lo, 1)

                def step(h, q):
                    parts = step_parts(h, q)
                    i = NB * h + q
                    before = parts["before"] and (parts["score"] or q < 1)
                    if before:
                        inverse_sums(h, q, i - 1, (q - 1) % 2)
                    if parts["score"]:
                        maximum(h, q, 0)
                    if parts["weights"] and (parts["score"] or q < 2):
                        for c in range(NC):
                            take_lo(h, q, "w", c)
                    if parts["score"]:
                        maximum(h, q, 1)
                    if before:
                        dve.wait_ge(p1_scaled, i)
                        a = p0[:, (q - 1) % 4]
                        dve.scalar_tensor_tensor(out=a, in0=a, scalar=inv_sum[:, (q - 1) % 2, 0:1],
                                                 in1=p1[:, (q - 1) % 2], op0=ALU.mult,
                                                 op1=ALU.add).then_inc(weights, 1)
                    if parts["score"] and q in (2, 3):
                        for part in range(2):
                            take_lo(h, q, "v", 2 * (q - 2) + part)
                run(dve, step)

            @block.gpsimd
            def _(pool):
                pool.wait_ge(lam["done"], 2)

                def step(h, q):
                    parts = step_parts(h, q)
                    if not (parts["before"] and (parts["score"] or q < 1)):
                        return
                    b = p1[:, (q - 1) % 2]
                    hold(pool, pool_held, inverses, NB * h + q)
                    pool.tensor_scalar(b, b, inv_sum[:, (q - 1) % 2, 1:2], lam["neg"][:, 0:1],
                                       ALU.mult, ALU.mult).then_inc(p1_scaled, 1)
                run(pool, step)



def attend_sample(nc, qk_hi, qk_lo, v_dram, o_dram, consts, lam_vectors):
    S, NB, T0 = S_SAMPLE, S_SAMPLE // P, S_PROMPT
    with ExitStack() as stack:
        m = Memory(nc, stack, "sa")
        ka = m.sb("ka", [P, 2, 2, S], F32R)
        kb = m.sb("kb", [HD + ALIBI, 2, 2, S], F32R)
        qa = m.sb("qa", [P, 2, 2, S], F32R)
        qb = m.sb("qb", [HD + ALIBI, 2, 2, S], F32R)
        diag = m.sb("diag", [P, 2, P], F32R)
        vt = m.sb("vt", [P, 2, S])
        vh = m.sb("vh", [P, 2, NB, P], F32R)
        vl = m.sb("vl", [P, 2, NB, P], F32R)
        p0 = m.sb("p0", [P, 2, NB, S])
        p1 = m.sb("p1", [P, 2, NB, S])
        wth = m.sb("wth", [P, 2, NB, S], F32R)
        wtl = m.sb("wtl", [P, 2, NB, S], F32R)
        o_out = m.sb("o_out", [P, 2, S])
        row_max = m.sb("row_max", [P, 2, 4])
        neg_max = m.sb("neg_max", [P, 2, 4])
        row_sum = m.sb("row_sum", [P, 2, 4])
        inv_sum = m.sb("inv_sum", [P, 2, 4])
        ident = m.sb("ident", [P, P])
        ident_r = m.sb("ident_r", [P, P], F32R)
        score = m.ps("score", [P, 2, 2, GROUP])
        turned_w = m.ps("turned_w", [P, GROUP])
        turned_v = m.ps("turned_v", [P, S])
        o_acc = m.ps("o_acc", [P, S])

        consts_in = m.sem("consts_in")
        head_in = [m.sem(f"head_in{n}") for n in range(2)]
        scores = m.sem("scores")
        maxed = m.sem("maxed")
        maxima = m.sem("maxima")
        exps = m.sem("exps")
        inverses = m.sem("inverses")
        p1_scaled = m.sem("p1_scaled")
        weights = m.sem("weights")
        v_turned = m.sem("v_turned")
        v_hi = m.sem("v_hi")
        v_lo = m.sem("v_lo")
        w_turned = m.sem("w_turned")
        w_hi = m.sem("w_hi")
        w_lo = m.sem("w_lo")
        o_done = m.sem("o_done")
        o_copied = m.sem("o_copied")
        o_stored = [m.sem(f"o_stored{n}") for n in range(2)]
        lam = load_lambda(m, m.sem("lam_in"))

        with nc.Block() as block:
            @block.sync
            def _(sp):
                sp.dma_start(ident[:], consts["ident"]).then_inc(consts_in, 16)
                sp.dma_start(f32(ident_r[:]), consts["ident"]).then_inc(consts_in, 16)
                for s in range(2):
                    for n in range(2):
                        sp.dma_start(f32(kb[HD:, s, n]), consts["position"][:, 0:S]).then_inc(consts_in, 16)
                lambda_load(sp, lam, lam_vectors)

                def store(h):
                    sp.wait_ge(o_copied, h + 1)
                    sp.dma_start(o_dram[h, :, T0:T], o_out[:, h % 2]).then_inc(o_stored[h % 2], 16)

                for h in range(HEADS):
                    s = h % 2
                    wait(sp, scores, h - 1)
                    wait(sp, v_turned, h - 1)
                    for n in range(2):
                        rows = slice(HD * n, HD * n + HD)
                        for dst, src, head in ((ka[0:HD, s, n], qk_hi, HEADS + h), (ka[HD:, s, n], qk_hi, HEADS + h),
                                               (kb[0:HD, s, n], qk_lo, HEADS + h), (qa[0:HD, s, n], qk_hi, h),
                                               (qa[HD:, s, n], qk_lo, h), (qb[0:HD, s, n], qk_hi, h)):
                            sp.dma_start(f32(dst), src[head, rows, T0:T]).then_inc(head_in[s], 16)
                        sp.dma_start(f32(qb[HD:, s, n]), consts["penalty"][h, :, 0:S]).then_inc(head_in[s], 16)
                    sp.dma_start(f32(diag[:, s]), consts["diag"][h]).then_inc(head_in[s], 16)
                    sp.dma_start(vt[:, s], v_dram[h, :, T0:T]).then_inc(head_in[s], 16)
                    if h >= 2:
                        store(h - 2)
                for h in range(HEADS - 2, HEADS):
                    store(h)
                for s in range(2):
                    sp.wait_ge(o_stored[s], 16 * HEADS // 2)

            @block.tensor
            def _(pe):
                pe.wait_ge(consts_in, 96)
                for h in range(HEADS + 1):
                    s = h % 2
                    if h < HEADS:
                        pe.wait_ge(head_in[s], 256 * (h // 2 + 1))
                        wait(pe, exps, 4 * (h - 1))
                        for n in range(2):
                            for q in range(NB):
                                out = score[:, s, n, q * S:(q + 1) * S]
                                at = slice(q * P, (q + 1) * P)
                                pe.matmul(out, qa[:, s, n, at], ka[:, s, n], start=True, stop=False)
                                pe.matmul(out[:, at], ident_r[:], diag[:, s], start=False, stop=False)
                                mm = pe.matmul(out, qb[:, s, n, at], kb[:, s, n], start=False, stop=True)
                        mm.then_inc(scores, 1)
                        wait(pe, v_lo, h)
                        for k in range(NB):
                            mm = pe.transpose(turned_v[:, k * P:(k + 1) * P], vt[:, s, k * P:(k + 1) * P], ident[:])
                        mm.then_inc(v_turned, 1)
                    if h >= 1:
                        g, s = h - 1, (h - 1) % 2
                        pe.wait_ge(weights, 2 * g + 2)
                        wait(pe, w_lo, g)
                        for k in range(NB):
                            for q in range(NB):
                                mm = pe.transpose(turned_w[:, (NB * k + q) * P:(NB * k + q + 1) * P],
                                                  p0[:, s, q, k * P:(k + 1) * P], ident[:])
                        mm.then_inc(w_turned, 1)
                        pe.wait_ge(w_lo, g + 1)
                        pe.wait_ge(v_lo, g + 1)
                        wait(pe, o_copied, g)
                        three_pass(pe, o_acc[:], lambda k: vh[:, s, k], lambda k: vl[:, s, k],
                                   lambda k: wth[:, s, k], lambda k: wtl[:, s, k], range(NB)).then_inc(o_done, 1)

            @block.scalar
            def _(act):
                lambda_exps(act, lam)
                for h in range(HEADS + 1):
                    s = h % 2
                    if h < HEADS:
                        act.wait_ge(v_turned, h + 1)
                        wait(act, o_done, h - 1)
                        act.activation(vh[:, s].rearrange("p k t -> p (k t)"), turned_v[:], ACT.Copy).then_inc(v_hi, 1)
                        act.wait_ge(maxima, h + 1)
                        wait(act, w_turned, h - 1)
                        for n, p in enumerate((p0, p1)):
                            for q in range(NB):
                                x = NB * n + q
                                act.activation(p[:, s, q], score[:, s, n, q * S:(q + 1) * S], ACT.Exp,
                                               bias=neg_max[:, s, x:x + 1], scale=SCALE,
                                               accum_out=row_sum[:, s, x:x + 1]).then_inc(exps, 1)
                    if h >= 1:
                        g, s = h - 1, (h - 1) % 2
                        act.wait_ge(w_turned, g + 1)
                        act.activation(wth[:, s].rearrange("p k t -> p (k t)"), turned_w[:], ACT.Copy).then_inc(w_hi, 1)
                        act.wait_ge(o_done, g + 1)
                        wait(act, o_stored[s], 16 * (g // 2))
                        act.activation(o_out[:, s], o_acc[:], ACT.Copy).then_inc(o_copied, 1)

            @block.vector
            def _(dve):
                lambda_dots(dve, lam)
                lambda_negative(dve, lam)
                for h in range(HEADS + 1):
                    s = h % 2
                    if h < HEADS:
                        dve.wait_ge(v_hi, h + 1)
                        dve.tensor_tensor(vl[:, s].rearrange("p k t -> p (k t)"), turned_v[:],
                                          f32(vh[:, s].rearrange("p k t -> p (k t)")), ALU.subtract).then_inc(v_lo, 1)
                        dve.wait_ge(scores, h + 1)
                        dve.tensor_reduce(row_max[:, s], score[:, s].rearrange("p n (q t) -> p (n q) t", q=NB),
                                          AX_X, ALU.max).then_inc(maxed, 1)
                        dve.wait_ge(maxed, h + 1)
                        dve.tensor_scalar(neg_max[:, s], row_max[:, s], -SCALE, None, ALU.mult).then_inc(maxima, 1)
                    if h >= 1:
                        g, s = h - 1, (h - 1) % 2
                        for q in range(NB):
                            dve.wait_ge(p1_scaled, 2 * g + q + 1)
                            dve.scalar_tensor_tensor(out=p0[:, s, q], in0=p0[:, s, q], scalar=inv_sum[:, s, q:q + 1],
                                                     in1=p1[:, s, q], op0=ALU.mult, op1=ALU.add).then_inc(weights, 1)
                        dve.wait_ge(w_hi, g + 1)
                        dve.tensor_tensor(wtl[:, s].rearrange("p k t -> p (k t)"), turned_w[:],
                                          f32(wth[:, s].rearrange("p k t -> p (k t)")), ALU.subtract).then_inc(w_lo, 1)
                    if h < HEADS:
                        s = h % 2
                        dve.wait_ge(exps, 4 * h + 4)
                        dve.reciprocal(inv_sum[:, s], row_sum[:, s]).then_inc(inverses, 1)

            @block.gpsimd
            def _(pool):
                pool.wait_ge(lam["done"], 2)
                for h in range(HEADS):
                    s = h % 2
                    pool.wait_ge(inverses, h + 1)
                    for q in range(NB):
                        pool.tensor_scalar(p1[:, s, q], p1[:, s, q], inv_sum[:, s, NB + q:NB + q + 1],
                                           lam["neg"][:, 0:1], ALU.mult, ALU.mult).then_inc(p1_scaled, 1)



WIDE = 384


def project_out(nc, tag, w_dram, branch, gate, residuals, ident_dram, out, subln=None, final_norm=None):
    NGR = T // WIDE
    TT = WIDE // P
    with ExitStack() as stack:
        m = Memory(nc, stack, tag)
        raw = m.sb("raw", [P, 2, D])
        wg = m.sb("wg", [P, D])
        wh = m.sb("wh", [P, KB, D], F32R)
        wl = m.sb("wl", [P, KB, D], F32R)
        row_w = m.sb("row_w", [P, 1])
        ones = m.sb("ones", [P, P])
        eps = m.sb("eps", [P, 2])
        b_in = m.sb("b_in", [P, 2, WIDE])
        g_in = m.sb("g_in", [P, 2, WIDE])
        if subln is not None:
            sq = m.sb("sq", [P, 2, WIDE])
            inv = m.sb("inv", [P, 2, WIDE])
            normed = m.sb("normed", [P, 2, WIDE])
        act_in = m.sb("act_in", [P, 2, WIDE])
        ah = m.sb("ah", [P, 2, KB, WIDE], F32R)
        al = m.sb("al", [P, 2, KB, WIDE], F32R)
        res = m.sb("res", [P, 2, len(residuals), WIDE])
        acc = m.ps("acc", [P, 4, GROUP])
        sums = m.ps("sums", [P, 2, GROUP])

        weights_in = [m.sem(f"weights_in{s}") for s in range(2)]
        consts_in = m.sem("consts_in")
        consts_set = m.sem("consts_set")
        w_scaled = m.sem("w_scaled")
        w_hi = m.sem("w_hi")
        w_lo = m.sem("w_lo")
        unit_in = [m.sem(f"unit_in{s}") for s in range(2)]
        squared = m.sem("squared")
        summed = m.sem("summed")
        rooted = m.sem("rooted")
        inverted = m.sem("inverted")
        normalised = m.sem("normalised")
        gated = m.sem("gated")
        a_hi = m.sem("a_hi")
        a_lo = m.sem("a_lo")
        products = m.sem("products")
        res_in = [m.sem(f"res_in{s}") for s in range(2)]
        added = m.sem("added")
        stored = [m.sem(f"stored{s}") for s in range(2)]
        if final_norm is None:
            x_out = m.sb("x_out", [P, 2, WIDE])
            tmp = m.sb("tmp", [P, 2, WIDE])
            half_added = m.sem("half_added")
        else:
            fn = m.sb("fn", [P, KB])
            x2 = m.sb("x2", [P, 2, WIDE])
            x2g = m.sb("x2g", [P, 2, KB, WIDE])
            x2sq = m.sb("x2sq", [P, 2, WIDE])
            total = m.sb("total", [P, 2, WIDE])
            root = m.sb("root", [P, 2, TT])
            rstd = m.sb("rstd", [P, 2, TT])
            rows = m.sb("rows", [P, 2, D])
            ident = m.sb("ident", [P, P])
            turned = m.ps("turned", [P, 2, GROUP])
            x2_scaled = m.sem("x2_scaled")
            x2_squared = m.sem("x2_squared")
            totals = m.sem("totals")
            token_sums = m.sem("token_sums")
            token_roots = m.sem("token_roots")
            token_inv = m.sem("token_inv")
            turns = m.sem("turns")
            rows_done = m.sem("rows_done")

        def run(eng, step):
            step(0, 0)
            step(1, 1)
            with eng.Fori(1, NGR // 2) as j:
                for s in range(2):
                    step(2 * j + s, s)
            step(NGR, 0)
            step(NGR + 1, 1)

        def has(i):
            full = not isinstance(i, int)
            return (full or i < NGR, full or 1 <= i <= NGR, final_norm is not None and (full or i >= 2))

        def cols(src, k, g):
            return src[k, :, bass.ds(g * WIDE, WIDE)]

        with nc.Block() as block:
            @block.sync
            def _(sp):
                if subln is not None:
                    sp.dma_start(row_w[:], subln).then_inc(consts_in, 16)
                if final_norm is not None:
                    sp.dma_start(ident[:], ident_dram).then_inc(consts_in, 16)
                    sp.dma_start(fn[:], final_norm).then_inc(consts_in, 16)
                for k in range(KB):
                    wait(sp, w_scaled, k - 1)
                    wait(sp, w_hi, k - 1)
                    sp.dma_start(raw[:, k % 2], w_dram[0, k * P:(k + 1) * P, :]).then_inc(weights_in[k % 2], 16)

                def step(i, s):
                    prep, mult, finish = has(i)
                    for k in range(KB):
                        if prep:
                            n = KB * i + k
                            wait(sp, gated, n - 1)
                            sp.dma_start(b_in[:, k % 2], cols(branch, k, i)).then_inc(unit_in[k % 2], 16)
                            sp.dma_start(g_in[:, k % 2], cols(gate, k, i)).then_inc(unit_in[k % 2], 16)
                        if mult:
                            n = KB * (i - 1) + k
                            wait(sp, added, n - 1)
                            for r, src in enumerate(residuals):
                                sp.dma_start(res[:, k % 2, r], cols(src, k, i - 1)).then_inc(res_in[k % 2], 16)
                            if final_norm is None and not (isinstance(n, int) and n == 0):
                                sp.wait_ge(added, n)
                                kk, g = ((k - 1) % KB, i - 1 if k else i - 2)
                                sp.dma_start(cols(out, kk, g), x_out[:, kk % 2]).then_inc(stored[kk % 2], 16)
                        if finish and k % 2 == 0 and 0 < k <= 2 * TT:
                            tt = k // 2 - 1
                            sp.wait_ge(rows_done, 2 * (TT * (i - 2) + tt) + 4)
                            dst, at = finish_rows(i, tt)
                            sp.dma_start(dst[at, :], rows[:, (TT * s + tt) % 2]).then_inc(stored[(TT * s + tt) % 2], 16)
                    if final_norm is None and isinstance(i, int) and i == NGR:
                        sp.wait_ge(added, KB * NGR)
                        sp.dma_start(cols(out, KB - 1, NGR - 1), x_out[:, 1]).then_inc(stored[1], 16)

                def finish_rows(i, tt):
                    if isinstance(i, int):
                        tok = (i - 2) * WIDE + tt * P
                        return (out[0], slice(tok, tok + P)) if tok < S_PROMPT else \
                            (out[1], slice(tok - S_PROMPT, tok - S_PROMPT + P))
                    return out[0], bass.ds((i - 2) * WIDE + tt * P, P)
                run(sp, step)
                each = KB * NGR // 2 if final_norm is None else NT // 2
                for s in range(2):
                    sp.wait_ge(stored[s], 16 * each)

            @block.gpsimd
            def _(pool):
                held = m.sem("pool_held")

                def step(i, s):
                    if not has(i)[0]:
                        return
                    for k in range(KB):
                        n = KB * i + k
                        if subln is not None:
                            pool.wait_ge(normalised, n + 1)
                        else:
                            pool.wait_ge(unit_in[k % 2], 32 * (KB // 2 * i + k // 2 + 1))
                        wait(pool, a_hi, n - 1)
                        wait(pool, a_lo, n - 1)
                        pool.tensor_tensor(act_in[:, k % 2], normed[:, k % 2] if subln is not None else b_in[:, k % 2],
                                           g_in[:, k % 2], ALU.mult).then_inc(gated, 1)
                        pool.wait_ge(a_hi, n + 1)
                        pool.tensor_tensor(al[:, s, k], act_in[:, k % 2], f32(ah[:, s, k]),
                                           ALU.subtract).then_inc(a_lo, 1)
                run(pool, step)

            @block.tensor
            def _(pe):
                pe.wait_ge(consts_set, 3)
                if final_norm is not None:
                    pe.wait_ge(consts_in, 32)

                def token_sum(i, s):
                    pe.wait_ge(totals, KB * (i - 1))
                    wait(pe, token_roots, i - 2)
                    for tt in range(TT):
                        mm = pe.matmul(sums[:, 0, 2 * tt:2 * tt + 2], total[:, s, tt * P:(tt + 1) * P],
                                       ones[:, 0:2], start=True, stop=True)
                    mm.then_inc(token_sums, 1)

                def turn(i, s, n):
                    tt, half = divmod(n, 2)
                    u = 2 * TT * (i - 2) + n
                    if n == 0:
                        pe.wait_ge(x2_scaled, KB * (i - 1))
                    pe.wait_ge(rows_done, u + 1)
                    for x in range(4):
                        mm = pe.transpose(turned[:, n % 2, x * P:(x + 1) * P],
                                          x2g[:, s, 4 * half + x, tt * P:(tt + 1) * P], ident[:])
                    mm.then_inc(turns, 1)

                def step(i, s):
                    prep, mult, finish = has(i)
                    if finish:
                        token_sum(i, s)
                    for k in range(KB):
                        if mult:
                            n = KB * (i - 1) + k
                            if k == 0:
                                pe.wait_ge(a_lo, KB * i)
                            if isinstance(i, int) and i == 1:
                                pe.wait_ge(w_lo, KB)
                            wait(pe, added, n - 3)
                            o = 1 - s
                            three_pass(pe, acc[:, k % 4, :WIDE], lambda x: wh[:, x, k * P:(k + 1) * P],
                                       lambda x: wl[:, x, k * P:(k + 1) * P], lambda x: ah[:, o, x],
                                       lambda x: al[:, o, x], range(KB)).then_inc(products, 1)
                        if finish and k < 2 * TT:
                            turn(i, s, k)
                        if prep and subln is not None:
                            n = KB * i + k
                            pe.wait_ge(squared, n + 1)
                            wait(pe, rooted, n - 1)
                            pe.matmul(sums[:, k % 2, :WIDE], ones[:], sq[:, k % 2], start=True,
                                      stop=True).then_inc(summed, 1)
                run(pe, step)

            @block.scalar
            def _(act):
                act.wait_ge(consts_set, 3)
                for k in range(KB):
                    act.wait_ge(weights_in[k % 2], 16 * (k // 2 + 1))
                    act.activation(wh[:, k], raw[:, k % 2], ACT.Copy, scale=row_w[:, 0:1]).then_inc(w_hi, 1)
                if final_norm is not None:
                    act.wait_ge(consts_in, 32)

                def square(i, k):
                    n = KB * i + k
                    act.wait_ge(unit_in[k % 2], 32 * (KB // 2 * i + k // 2 + 1))
                    wait(act, summed, n - 1)
                    act.activation(sq[:, k % 2], b_in[:, k % 2], ACT.Square).then_inc(squared, 1)

                def step(i, s):
                    prep, mult, finish = has(i)
                    if finish:
                        act.wait_ge(token_sums, i - 1)
                        act.activation(root[:, s], sums[:, 0, 0:2 * TT:2], ACT.Sqrt, bias=eps[:, 1:2],
                                       scale=1.0 / D).then_inc(token_roots, 1)
                    for k in range(KB):
                        n = KB * i + k
                        if prep and subln is not None:
                            square(i, k)
                            act.wait_ge(summed, n + 1)
                            wait(act, normalised, n - 1)
                            act.activation(inv[:, k % 2], sums[:, k % 2, :WIDE], ACT.Sqrt, bias=eps[:, 0:1],
                                           scale=1.0 / P).then_inc(rooted, 1)
                        if prep:
                            act.wait_ge(gated, n + 1)
                            if k == 0:
                                wait(act, products, KB * (i - 1))
                            act.activation(ah[:, s, k], act_in[:, k % 2], ACT.Copy).then_inc(a_hi, 1)
                        if mult and final_norm is not None:
                            o = 1 - s
                            act.wait_ge(added, KB * (i - 1) + k + 1)
                            if k == 0:
                                wait(act, turns, 2 * TT * (i - 2))
                            act.activation(x2g[:, o, k], x2[:, k % 2], ACT.Copy, scale=fn[:, k:k + 1]).then_inc(x2_scaled, 1)
                            wait(act, totals, KB * (i - 1) + k - 1)
                            act.activation(x2sq[:, k % 2], x2[:, k % 2], ACT.Square).then_inc(x2_squared, 1)
                run(act, step)

            @block.vector
            def _(dve):
                dve.memset(ones[:], 1.0).then_inc(consts_set, 1)
                dve.memset(eps[:, 0:1], SUBLN_EPS).then_inc(consts_set, 1)
                if subln is None:
                    dve.memset(row_w[:], 1.0).then_inc(consts_set, 1)
                else:
                    dve.wait_ge(consts_in, 16)
                    dve.tensor_scalar(row_w[:], row_w[:], 1.0 - LAM_INIT, None, ALU.mult).then_inc(consts_set, 1)
                dve.memset(eps[:, 1:2], EPS).then_inc(consts_set, 1)
                dve.wait_ge(consts_set, 4)
                if final_norm is not None:
                    dve.sem_inc(rows_done, 2)
                for k in range(KB):
                    dve.wait_ge(weights_in[k % 2], 16 * (k // 2 + 1))
                    wait(dve, w_lo, k)
                    dve.tensor_scalar(wg[:], raw[:, k % 2], row_w[:, 0:1], None, ALU.mult).then_inc(w_scaled, 1)
                    dve.wait_ge(w_hi, k + 1)
                    dve.wait_ge(w_scaled, k + 1)
                    dve.tensor_tensor(wl[:, k], wg[:], f32(wh[:, k]), ALU.subtract).then_inc(w_lo, 1)

                def rows_out(i, s, n):
                    tt, half = divmod(n, 2)
                    tile = TT * (i - 2) + tt
                    slot = (TT * s + tt) % 2
                    dve.wait_ge(turns, 2 * TT * (i - 2) + n + 1)
                    if half == 0:
                        before = 3 * ((i - 2) // 2) if isinstance(i, int) else (i - 2 - s) // 2 * 3
                        wait(dve, stored[slot], 16 * (before + (TT * s + tt) // 2))
                    dve.tensor_scalar(rows[:, slot, half * GROUP:(half + 1) * GROUP], turned[:, n % 2],
                                      rstd[:, s, tt:tt + 1], None, ALU.mult).then_inc(rows_done, 1)

                def step(i, s):
                    prep, mult, finish = has(i)
                    if finish:
                        dve.wait_ge(token_roots, i - 1)
                        dve.reciprocal(rstd[:, s], root[:, s]).then_inc(token_inv, 1)
                    for k in range(KB):
                        if prep and subln is not None:
                            n = KB * i + k
                            dve.wait_ge(rooted, n + 1)
                            dve.reciprocal(inv[:, k % 2], inv[:, k % 2]).then_inc(inverted, 1)
                            dve.wait_ge(inverted, n + 1)
                            wait(dve, gated, n - 1)
                            dve.tensor_tensor(normed[:, k % 2], b_in[:, k % 2], inv[:, k % 2],
                                              ALU.mult).then_inc(normalised, 1)
                        if mult:
                            n = KB * (i - 1) + k
                            o = 1 - s
                            dve.wait_ge(products, n + 1)
                            dve.wait_ge(res_in[k % 2], 16 * len(residuals) * (KB // 2 * (i - 1) + k // 2 + 1))
                            src = acc[:, k % 4, :WIDE]
                            if final_norm is None:
                                dve.tensor_tensor(tmp[:, k % 2], src, res[:, k % 2, 0], ALU.add).then_inc(half_added, 1)
                                dve.wait_ge(half_added, n + 1)
                                wait(dve, stored[k % 2], 16 * (KB // 2 * (i - 1) + k // 2))
                                dve.tensor_tensor(x_out[:, k % 2], tmp[:, k % 2], res[:, k % 2, 1],
                                                  ALU.add).then_inc(added, 1)
                            else:
                                wait(dve, x2_squared, n - 1)
                                dve.tensor_tensor(x2[:, k % 2], src, res[:, k % 2, 0], ALU.add).then_inc(added, 1)
                                dve.wait_ge(x2_squared, n + 1)
                                if k == 0:
                                    wait(dve, token_sums, i - 2)
                                    dve.tensor_copy(total[:, o], x2sq[:, 0]).then_inc(totals, 1)
                                else:
                                    dve.wait_ge(totals, n)
                                    dve.tensor_tensor(total[:, o], total[:, o], x2sq[:, k % 2], ALU.add).then_inc(totals, 1)
                        if finish and k < 2 * TT:
                            if k == 0:
                                dve.wait_ge(token_inv, i - 1)
                            rows_out(i, s, k)
                run(dve, step)



def round12(a):
    def cut(x):
        m, e = np.frexp(x)
        return np.ldexp(np.rint(m * 4096) / 4096, e)
    hi = cut(a)
    return hi.astype(np.float32), cut(a - hi).astype(np.float32)


def fourier_constants():
    c = np.arange(P)
    turn = 2 * np.pi * np.outer(c, c) / P
    out = {}
    out["chan"] = np.stack(round12(np.concatenate([np.cos(turn), np.sin(turn)], 1)))
    S, H = S_PROMPT, S_PROMPT // 4
    norm = 1.0 / math.sqrt(S * P)
    t, k = np.arange(H)[:, None], np.arange(H)[None, :]
    alt = (-1.0) ** np.arange(H)
    odd_sin = np.sin(np.pi * (2 * k + 1) * t / (S // 2))
    odd_sin[0] = alt
    kinds = np.stack([np.cos(2 * np.pi * k * t / (S // 2)), np.cos(np.pi * (2 * k + 1) * t / (S // 2)),
                      np.sin(2 * np.pi * k * t / (S // 2)), odd_sin]) * norm
    out["time"] = np.stack(round12(kinds))
    extra = np.zeros((P, H))
    extra[0] = alt * norm
    out["extra"] = extra.astype(np.float32)
    nyq = np.zeros((5, P, 2))
    nyq[:4] = (alt * norm).reshape(4, P, 1)
    nyq[4, 0] = norm
    out["nyquist"] = np.ascontiguousarray(nyq.transpose(1, 0, 2)).astype(np.float32)
    S = S_SAMPLE
    t = np.arange(S)
    turn = 2 * np.pi * np.outer(t, t) / S
    out["short"] = np.stack(round12(np.stack([np.cos(turn), -np.sin(turn)]) / math.sqrt(S * P)))
    return {k: np.ascontiguousarray(v) for k, v in out.items()}


def fourier_prompt(nc, u_dram, f_dram, consts):
    S, H = S_PROMPT, S_PROMPT // 4
    TB = H // P
    NBK = 4 * TB + 1
    UN = (NBK + 3) // 4
    EXTRA = 4 * TB
    with ExitStack() as stack:
        m = Memory(nc, stack, "fp")
        th = m.sb("th", [P, 4, TB, H], F32R)
        tl = m.sb("tl", [P, 4, TB, H], F32R)
        extra = m.sb("extra", [P, H], F32R)
        nyq = m.sb("nyq", [P, TB + 1, 2], F32R)
        ch = m.sb("ch", [P, 2 * P], F32R)
        cl = m.sb("cl", [P, 2 * P], F32R)
        u = m.sb("u", [P, 2, S])
        even = m.sb("even", [P, S // 2 + 1])
        odd = m.sb("odd", [P, S // 2])
        fold = m.sb("fold", [P, NBK, P])
        fh = m.sb("fh", [P, NBK, P], F32R)
        fl = m.sb("fl", [P, NBK, P], F32R)
        ah = m.sb("ah", [P, 2, NBK, P], F32R)
        al = m.sb("al", [P, 2, NBK, P], F32R)
        xs = m.sb("xs", [P, 2, H])
        f = m.sb("f", [P, 2, S])
        chan = m.ps("chan", [P, 2, GROUP])
        time = m.ps("time", [P, 4, H])
        ny = m.ps("ny", [P, 2])

        sp_held = m.sem("sp_held")
        consts_in = m.sem("consts_in")
        zeroed = m.sem("zeroed")
        u_in = [m.sem(f"u_in{s}") for s in range(2)]
        ends = m.sem("ends")
        halves = m.sem("halves")
        mids = m.sem("mids")
        folds = m.sem("folds")
        f_hi = m.sem("f_hi")
        f_lo = m.sem("f_lo")
        chans = m.sem("chans")
        c_hi = m.sem("c_hi")
        c_lo = m.sem("c_lo")
        times = m.sem("times")
        x_copied = m.sem("x_copied")
        f_done = m.sem("f_done")
        stored = [m.sem(f"stored{s}") for s in range(2)]

        def run(eng, step):
            step(0, 0)
            with eng.Fori(0, HEADS // 2 - 1) as j:
                step(2 * j + 1, 1)
                step(2 * j + 2, 0)
            step(HEADS - 1, 1)
            step(HEADS, 0)

        def first(i):
            return not isinstance(i, int) or i < HEADS

        def second(i):
            return not isinstance(i, int) or i >= 1

        with nc.Block() as block:
            @block.sync
            def _(sp):
                def load(i, s):
                    if first(i):
                        if not isinstance(i, int):
                            hold(sp, sp_held, ends, i - 1)
                            hold(sp, sp_held, halves, 2 * (i - 1))
                        else:
                            wait(sp, ends, i - 1)
                            wait(sp, halves, 2 * (i - 1))
                        sp.dma_start(u[:, s], u_dram[bass.ds(i, 1), :, 0:S].rearrange("a p t -> p (a t)")).then_inc(u_in[s], 16)
                load(0, 0)
                for dst, src in ((ch, consts["chan"][0]), (cl, consts["chan"][1])):
                    sp.dma_start(f32(dst[:]), src).then_inc(consts_in, 16)
                for kind in range(4):
                    for dst, part in ((th, 0), (tl, 1)):
                        sp.dma_start(f32(dst[:, kind]),
                                     consts["time"][part, kind].rearrange("(b p) k -> p b k", p=P)).then_inc(consts_in, 16)
                sp.dma_start(f32(extra[:]), consts["extra"]).then_inc(consts_in, 16)
                sp.dma_start(f32(nyq[:]), consts["nyquist"]).then_inc(consts_in, 16)

                def step(i, s):
                    if not (isinstance(i, int) and i == 0):
                        load(i, s)
                    if second(i):
                        hold(sp, sp_held, f_done, 4 * i)
                        sp.dma_start(f_dram[bass.ds(i - 1, 1), :, 0:S].rearrange("a p t -> p (a t)"),
                                     f[:, 1 - s]).then_inc(stored[1 - s], 16)
                run(sp, step)
                for s in range(2):
                    sp.wait_ge(stored[s], 16 * HEADS // 2)

            @block.tensor
            def _(pe):
                pe.wait_ge(consts_in, 16 * 12)

                def step(i, s):
                    if first(i):
                        pe.wait_ge(f_lo, i + 1)
                        for n in range(UN):
                            wait(pe, c_lo, UN * i + n - 1)
                            for b in range(4 * n, min(4 * n + 4, NBK)):
                                cos = b < 2 * TB or b == EXTRA
                                part = slice(0, P) if cos else slice(P, 2 * P)
                                mm = three_pass(pe, chan[:, (UN * s + n) % 2, (b % 4) * P:(b % 4 + 1) * P],
                                                lambda k: fh[:, b], lambda k: fl[:, b],
                                                lambda k: ch[:, part], lambda k: cl[:, part], range(1))
                            mm.then_inc(chans, 1)
                    if second(i):
                        o = 1 - s
                        pe.wait_ge(c_lo, UN * i)
                        wait(pe, x_copied, 3 * (i - 1))
                        for kind in range(2):
                            three_pass(pe, time[:, kind], lambda k: ah[:, o, TB * kind + k],
                                       lambda k: al[:, o, TB * kind + k], lambda k: th[:, kind, k],
                                       lambda k: tl[:, kind, k], range(TB), last=kind == 1)
                            if kind == 0:
                                pe.matmul(time[:, 0], ah[:, o, EXTRA], extra[:], start=False, stop=False)
                                pe.matmul(time[:, 0], al[:, o, EXTRA], extra[:], start=False, stop=True)
                        for n, b in enumerate([0, 1, 2, 3, EXTRA]):
                            pe.matmul(ny[:], ah[:, o, b], nyq[:, n], start=n == 0, stop=False)
                            mm = pe.matmul(ny[:], al[:, o, b], nyq[:, n], start=False, stop=b == EXTRA)
                        mm.then_inc(times, 1)
                        wait(pe, f_done, 4 * (i - 1))
                        for kind in (2, 3):
                            three_pass(pe, time[:, kind], lambda k: ah[:, o, TB * kind + k],
                                       lambda k: al[:, o, TB * kind + k], lambda k: th[:, kind, k],
                                       lambda k: tl[:, kind, k], range(TB)).then_inc(times, 1)
                run(pe, step)

            @block.scalar
            def _(act):
                def step(i, s):
                    if first(i):
                        act.wait_ge(u_in[s], 16 * (i // 2) + 16 if isinstance(i, int) else 16 * ((i - s) // 2) + 16)
                        wait(act, folds, 5 * i)
                        act.activation(even[:, 0:S // 2 + 1:S // 2], u[:, s, 0:S // 2 + 1:S // 2], ACT.Copy).then_inc(ends, 1)
                        act.wait_ge(folds, 5 * i + 5)
                        wait(act, chans, UN * i)
                        act.activation(fh[:], fold[:], ACT.Copy).then_inc(f_hi, 1)
                    if first(i):
                        for n in range(UN):
                            act.wait_ge(chans, UN * i + n + 1)
                            w = min(4, NBK - 4 * n)
                            act.activation(ah[:, s, 4 * n:4 * n + w].rearrange("p b t -> p (b t)"),
                                           chan[:, (UN * s + n) % 2, :w * P], ACT.Copy).then_inc(c_hi, 1)
                    if second(i):
                        o = 1 - s
                        act.wait_ge(times, 3 * (i - 1) + 1)
                        wait(act, f_done, 4 * (i - 1))
                        for kind in range(2):
                            act.activation(xs[:, kind], time[:, kind], ACT.Copy).then_inc(x_copied, 1)
                        before = (i - 1 - o) // 2
                        wait(act, stored[o], 16 * before)
                        act.activation(f[:, o, S // 2:S // 2 + 1], ny[:, 0:1], ACT.Copy).then_inc(x_copied, 1)
                run(act, step)

            @block.vector
            def _(dve):
                dve.memset(fold[:], 0.0).then_inc(zeroed, 1)
                dve.memset(odd[:], 0.0).then_inc(zeroed, 1)
                dve.wait_ge(zeroed, 2)

                def blocks(kind):
                    return fold[:, TB * kind:TB * kind + TB].rearrange("p b t -> p (b t)")

                def step(i, s):
                    half, quarter = S // 2, S // 4
                    if first(i):
                        dve.wait_ge(u_in[s], 16 * (i // 2) + 16 if isinstance(i, int) else 16 * ((i - s) // 2) + 16)
                        wait(dve, folds, 5 * i)
                        there, back = u[:, s, 1:half], u[:, s, S - 1:half:-1]
                        dve.tensor_tensor(even[:, 1:half], there, back, ALU.add).then_inc(halves, 1)
                        dve.tensor_tensor(odd[:, 1:half], there, back, ALU.subtract).then_inc(halves, 1)
                        dve.wait_ge(halves, 2 * i + 2)
                        dve.wait_ge(ends, i + 1)
                        wait(dve, f_lo, i)
                        near, far = even[:, 0:quarter], even[:, half:quarter:-1]
                        dve.tensor_tensor(blocks(0), near, far, ALU.add).then_inc(folds, 1)
                        dve.tensor_tensor(blocks(1), near, far, ALU.subtract).then_inc(folds, 1)
                        near, far = odd[:, 1:quarter], odd[:, half - 1:quarter:-1]
                        dve.tensor_tensor(blocks(2)[:, 1:], near, far, ALU.subtract).then_inc(folds, 1)
                        dve.tensor_tensor(blocks(3)[:, 1:], near, far, ALU.add).then_inc(folds, 1)
                        dve.tensor_copy(fold[:, EXTRA, 0:1], even[:, quarter:quarter + 1]).then_inc(mids, 1)
                        dve.tensor_copy(blocks(3)[:, 0:1], odd[:, quarter:quarter + 1]).then_inc(mids, 1)
                        dve.wait_ge(mids, 2 * i + 2)
                        dve.sem_inc(folds, 1)
                        dve.wait_ge(f_hi, i + 1)
                        dve.tensor_tensor(fl[:], fold[:], f32(fh[:]), ALU.subtract).then_inc(f_lo, 1)
                    if first(i):
                        for n in range(UN):
                            dve.wait_ge(c_hi, UN * i + n + 1)
                            w = min(4, NBK - 4 * n)
                            dve.tensor_tensor(al[:, s, 4 * n:4 * n + w].rearrange("p b t -> p (b t)"),
                                              chan[:, (UN * s + n) % 2, :w * P],
                                              f32(ah[:, s, 4 * n:4 * n + w].rearrange("p b t -> p (b t)")),
                                              ALU.subtract).then_inc(c_lo, 1)
                    if second(i):
                        o = 1 - s
                        g = f[:, o]
                        for n in range(2):
                            dve.wait_ge(x_copied, 3 * i)
                            dve.wait_ge(times, 3 * (i - 1) + 2 + n)
                            y = time[:, 2 + n]
                            dve.tensor_tensor(g[:, n:half:2], xs[:, n], y, ALU.subtract).then_inc(f_done, 1)
                            skip = 1 - n
                            dve.tensor_tensor(g[:, S - 2 + n:half:-2], xs[:, n, skip:], y[:, skip:],
                                              ALU.add).then_inc(f_done, 1)
                run(dve, step)


def fourier_sample(nc, u_dram, f_dram, consts):
    S, TB, T0 = S_SAMPLE, S_SAMPLE // P, S_PROMPT
    with ExitStack() as stack:
        m = Memory(nc, stack, "fs")
        th = m.sb("th", [P, 2, TB, S], F32R)
        tl = m.sb("tl", [P, 2, TB, S], F32R)
        ch = m.sb("ch", [P, 2 * P], F32R)
        cl = m.sb("cl", [P, 2 * P], F32R)
        u = m.sb("u", [P, HEADS, S])
        uh = m.sb("uh", [P, HEADS, S], F32R)
        ul = m.sb("ul", [P, HEADS, S], F32R)
        ah = m.sb("ah", [P, 2, TB, 2 * P], F32R)
        al = m.sb("al", [P, 2, TB, 2 * P], F32R)
        f = m.sb("f", [P, HEADS, S])
        chan = m.ps("chan", [P, 2, TB * 2 * P])
        out = m.ps("out", [P, 2, GROUP])
        consts_in, u_in, u_hi, u_lo = (m.sem(x) for x in ("consts_in", "u_in", "u_hi", "u_lo"))
        chans, c_hi, c_lo = (m.sem(x) for x in ("chans", "c_hi", "c_lo"))
        sums, copied, stored = (m.sem(x) for x in ("sums", "copied", "stored"))

        with nc.Block() as block:
            @block.sync
            def _(sp):
                sp.dma_start(u[:], u_dram[:, :, T0:T].rearrange("a p t -> p a t")).then_inc(u_in, 16)
                for dst, src in ((ch, consts["chan"][0]), (cl, consts["chan"][1])):
                    sp.dma_start(f32(dst[:]), src).then_inc(consts_in, 16)
                for kind in range(2):
                    for dst, part in ((th, 0), (tl, 1)):
                        sp.dma_start(f32(dst[:, kind]),
                                     consts["short"][part, kind].rearrange("(b p) k -> p b k", p=P)).then_inc(consts_in, 16)
                sp.wait_ge(copied, HEADS)
                sp.dma_start(f_dram[:, :, T0:T].rearrange("a p t -> p a t"), f[:]).then_inc(stored, 16)
                sp.wait_ge(stored, 16)

            @block.tensor
            def _(pe):
                pe.wait_ge(consts_in, 16 * 6)
                pe.wait_ge(u_lo, 1)
                for i in range(HEADS + 1):
                    s = i % 2
                    if i < HEADS:
                        wait(pe, c_lo, i - 1)
                        for b in range(TB):
                            at = slice(b * P, (b + 1) * P)
                            mm = three_pass(pe, chan[:, s, b * 2 * P:(b + 1) * 2 * P], lambda k: uh[:, i, at],
                                            lambda k: ul[:, i, at], lambda k: ch[:], lambda k: cl[:], range(1))
                        mm.then_inc(chans, 1)
                    if i >= 1:
                        o = 1 - s
                        pe.wait_ge(c_lo, i)
                        wait(pe, copied, i - 2)
                        three_pass(pe, out[:, o, :S], lambda x: ah[:, o, x // 2, (x % 2) * P:(x % 2 + 1) * P],
                                   lambda x: al[:, o, x // 2, (x % 2) * P:(x % 2 + 1) * P],
                                   lambda x: th[:, x % 2, x // 2], lambda x: tl[:, x % 2, x // 2],
                                   range(2 * TB)).then_inc(sums, 1)

            @block.scalar
            def _(act):
                act.wait_ge(u_in, 16)
                act.activation(uh[:], u[:], ACT.Copy).then_inc(u_hi, 1)
                for i in range(HEADS + 1):
                    if i < HEADS:
                        act.wait_ge(chans, i + 1)
                        wait(act, sums, i - 1)
                        act.activation(ah[:, i % 2].rearrange("p b c -> p (b c)"), chan[:, i % 2],
                                       ACT.Copy).then_inc(c_hi, 1)
                    if i >= 1:
                        act.wait_ge(sums, i)
                        act.activation(f[:, i - 1], out[:, (i - 1) % 2, :S], ACT.Copy).then_inc(copied, 1)

            @block.vector
            def _(dve):
                dve.wait_ge(u_hi, 1)
                dve.tensor_tensor(ul[:], u[:], f32(uh[:]), ALU.subtract).then_inc(u_lo, 1)
                for i in range(HEADS):
                    dve.wait_ge(c_hi, i + 1)
                    dve.tensor_tensor(al[:, i % 2].rearrange("p b c -> p (b c)"), chan[:, i % 2],
                                      f32(ah[:, i % 2].rearrange("p b c -> p (b c)")), ALU.subtract).then_inc(c_lo, 1)



def encoder(nc, x_prompt, x_sample, attn_norm, attn_w_in, lq1, lk1, lq2, lk2, attn_subln, attn_w_out,
            fnet_norm, fnet_w_in, fnet_w_out, final_norm, const_in, y_prompt, y_sample):
    def scratch(name, shape):
        return nc.dram_tensor(name, shape, F32, kind="Internal").ap()

    consts = {k: scratch(f"const_{k}", list(v.shape)) for k, v in const_in.items()}
    by_block = [KB, P, T]
    xh, xl = scratch("x_hi", by_block), scratch("x_lo", by_block)
    qk_hi, qk_lo = scratch("qk_hi", [2 * HEADS, P, T]), scratch("qk_lo", [2 * HEADS, P, T])
    v, attn_gate, o = scratch("v", by_block), scratch("attn_gate", by_block), scratch("o", by_block)
    x1 = scratch("x1", by_block)
    u, fnet_gate, f = scratch("u", by_block), scratch("fnet_gate", by_block), scratch("f", by_block)

    copied = nc.alloc_semaphore("consts_copied")
    with nc.Block() as block:
        @block.sync
        def _(sp):
            for k in const_in:
                sp.dma_start(consts[k], const_in[k]).then_inc(copied, 16)
            sp.wait_ge(copied, 16 * len(const_in))

    lam = (lq1, lk1, lq2, lk2)
    project_resident(nc, "ia", attn_w_in, attn_norm, const_in["ident"],
                     [(2 * HEADS, "split", (qk_hi, qk_lo)), (HEADS, "plain", (v,)), (HEADS, "silu", (attn_gate,))],
                     ("rows", x_prompt[0], x_sample[0]), spill=(xh, xl))
    attend_prompt(nc, qk_hi, qk_lo, v, o, consts, lam)
    attend_sample(nc, qk_hi, qk_lo, v, o, consts, lam)
    project_out(nc, "oa", attn_w_out, o, attn_gate, (xh, xl), const_in["ident"], x1, subln=attn_subln)
    project_resident(nc, "if", fnet_w_in, fnet_norm, const_in["ident"],
                     [(HEADS, "plain", (u,)), (HEADS, "silu", (fnet_gate,))], ("columns", x1))
    fourier_prompt(nc, u, f, consts)
    fourier_sample(nc, u, f, consts)
    project_out(nc, "of", fnet_w_out, f, fnet_gate, (x1,), const_in["ident"],
                (y_prompt[0], y_sample[0]), final_norm=final_norm)


def kernel(**inputs):
    import concourse.bacc as bacc
    from concourse.bass_utils import run_bass_kernel_spmd

    nc = bacc.Bacc("TRN2", target_bir_lowering=False, num_devices=1)
    arrays = {}

    def feed(name, a):
        a = np.ascontiguousarray(a)
        arrays[name] = a
        return nc.dram_tensor(name, a.shape, mybir.dt.from_np(a.dtype), kind="ExternalInput").ap()

    def columns(name, width):
        return feed(name, np.asarray(inputs[name]).reshape(width // P, P).T)

    plain = ("x_prompt", "x_sample", "attn_w_in", "attn_w_out", "fnet_w_in", "fnet_w_out",
             "attn_lambda_q1", "attn_lambda_k1", "attn_lambda_q2", "attn_lambda_k2")
    a = {n: feed(n, inputs[n]) for n in plain}
    const_in = {k: feed(f"table_{k}", v) for k, v in {**alibi_constants(), **fourier_constants()}.items()}
    outs = {n: nc.dram_tensor(n, s, F32, kind="ExternalOutput").ap()
            for n, s in (("y_prompt", [1, S_PROMPT, D]), ("y_sample", [1, S_SAMPLE, D]))}
    encoder(nc, a["x_prompt"], a["x_sample"], columns("attn_norm", D), a["attn_w_in"],
            a["attn_lambda_q1"], a["attn_lambda_k1"], a["attn_lambda_q2"], a["attn_lambda_k2"],
            columns("attn_subln", P), a["attn_w_out"], columns("fnet_norm", D), a["fnet_w_in"], a["fnet_w_out"],
            columns("final_norm", D), const_in, outs["y_prompt"], outs["y_sample"])
    r = run_bass_kernel_spmd(nc, [arrays], core_ids=[0])
    return tuple(r.results[0][n] for n in outs)
```
